# Optimizing a Trainium2 kernel written in Bass

```python
import jax, jax.numpy as jnp
from jax import lax
import numpy as np

D_MODEL = 1024
BATCH = 1
SEQ = 256
DEPTH = 2
DEC_BATCH = 1
DEC_SEQ = 64
PAST_LEN = 128

CHUNK = 64
PLE_DIM = 256
D_FF = 2816
EPS = 1e-6
GLA_HEADS = 4
GLA_DK = D_MODEL // 2 // GLA_HEADS
GLA_DV = D_MODEL // GLA_HEADS
GLA_RANK = 16
GLA_TAU = 16.0
SWA_HEADS = 16
SWA_KV_HEADS = 4
SWA_GROUP = SWA_HEADS // SWA_KV_HEADS
SWA_HD = D_MODEL // SWA_HEADS
WINDOW = 128
WIN_CHUNKS = WINDOW // CHUNK
SPLITS = (D_MODEL, D_MODEL,
          GLA_HEADS * GLA_DK, GLA_HEADS * GLA_DK, GLA_HEADS * GLA_DV, GLA_HEADS * GLA_DV, GLA_RANK,
          SWA_HEADS * SWA_HD, SWA_KV_HEADS * SWA_HD, SWA_KV_HEADS * SWA_HD)
D_IN = sum(SPLITS)

kernel_name = 'hybrid_gla_swa_sink_macaron_stream_step'

def rmsnorm(x, g):
    xf = x.astype(jnp.float32)
    y = xf * lax.rsqrt(jnp.mean(xf * xf, axis=-1, keepdims=True) + EPS)
    return (y * g.astype(jnp.float32)).astype(x.dtype)

def swiglu(x, w_up, w_down):
    gate, up = jnp.split(x @ w_up, 2, axis=-1)
    return (jax.nn.silu(gate) * up) @ w_down

def gla_scan(q, k, v, log_a, s0):
    B, L, H, DK = q.shape
    C = min(CHUNK, L)
    n = L // C

    def to_blocks(t):
        return jnp.moveaxis(t.reshape(B, n, C, H, t.shape[-1]), 1, 0)

    mask = jnp.tril(jnp.ones((C, C), dtype=bool))[None, :, :, None, None]

    def step(s, inp):
        qi, ki, vi, ai = inp
        b = jnp.cumsum(ai, axis=1)
        diff = b[:, :, None] - b[:, None, :]
        decay = jnp.where(mask, jnp.exp(jnp.where(mask, diff, 0.0)), 0.0)
        scores = jnp.einsum('bijhd,bjhd->bhij', qi[:, :, None] * decay, ki)
        o_intra = jnp.einsum('bhij,bjhv->bihv', scores, vi)
        o_inter = jnp.einsum('bihd,bhdv->bihv', qi * jnp.exp(b), s)
        b_last = b[:, -1]
        k_dec = ki * jnp.exp(b_last[:, None] - b)
        s_new = jnp.exp(b_last)[..., None] * s + jnp.einsum('bjhd,bjhv->bhdv', k_dec, vi)
        return s_new, o_intra + o_inter

    s_fin, o = lax.scan(step, s0, (to_blocks(q), to_blocks(k), to_blocks(v), to_blocks(log_a)))
    return jnp.moveaxis(o, 0, 1).reshape(B, L, H, v.shape[-1]), s_fin

def sink_attention(q, k, v, sinks, valid):
    sc = jnp.einsum('nihgd,njhd->nhgij', q, k).astype(jnp.float32) * SWA_HD ** -0.5
    if valid is not None:
        sc = jnp.where(valid[:, None, None, None, :], sc, -jnp.inf)
    sink = sinks.astype(jnp.float32).reshape(1, SWA_KV_HEADS, SWA_GROUP, 1, 1)
    m = jnp.maximum(sc.max(axis=-1, keepdims=True), sink)
    p = jnp.exp(sc - m)
    den = p.sum(axis=-1, keepdims=True) + jnp.exp(sink - m)
    return jnp.einsum('nhgij,njhd->nihgd', (p / den).astype(v.dtype), v)

def swa_prompt(q, k, v, sinks):
    B, S = q.shape[:2]
    n = S // CHUNK
    pad = WIN_CHUNKS * CHUNK

    def band(t):
        tp = jnp.pad(t, ((0, 0), (pad, 0), (0, 0), (0, 0))).reshape(B, n + WIN_CHUNKS, CHUNK, SWA_KV_HEADS, SWA_HD)
        kb = jnp.concatenate([tp[:, w:w + n] for w in range(WIN_CHUNKS + 1)], axis=2)
        return kb.reshape(B * n, (WIN_CHUNKS + 1) * CHUNK, SWA_KV_HEADS, SWA_HD)

    blk = jnp.repeat(jnp.arange(WIN_CHUNKS + 1), CHUNK)
    valid = (jnp.arange(n)[:, None] + blk[None, :] - WIN_CHUNKS) >= 0
    valid = jnp.tile(valid, (B, 1))
    qb = q.reshape(B * n, CHUNK, SWA_KV_HEADS, SWA_GROUP, SWA_HD)
    o = sink_attention(qb, band(k), band(v), sinks, valid)
    return o.reshape(B, S, SWA_HEADS * SWA_HD)

def layer(x, pe, s0, k_cache, v_cache, g_ffn1, w1_up, w1_down, g_mix, w_in, w_a2, b_a, g_gla,
          sinks, w_out, g_ffn2, w2_up, w2_down, g_ple, w_ple_gate, w_ple):
    B, L, _ = x.shape
    f32 = jnp.float32
    h = x + 0.5 * swiglu(rmsnorm(x, g_ffn1), w1_up, w1_down)
    u = rmsnorm(h, g_mix)
    idx = np.cumsum(SPLITS)[:-1].tolist()
    ga, gb, qa, ka, va, ra, alr, qb, kb, vb = jnp.split(u @ w_in, idx, axis=-1)
    log_a = jax.nn.log_sigmoid((alr @ w_a2 + b_a).astype(f32)) / GLA_TAU
    o_a, s_new = gla_scan(
        (qa.reshape(B, L, GLA_HEADS, GLA_DK) * GLA_DK ** -0.5).astype(f32),
        ka.reshape(B, L, GLA_HEADS, GLA_DK).astype(f32),
        va.reshape(B, L, GLA_HEADS, GLA_DV).astype(f32),
        log_a.reshape(B, L, GLA_HEADS, GLA_DK),
        s0.astype(f32))
    o_a = rmsnorm(o_a, g_gla.reshape(GLA_HEADS, GLA_DV)).astype(x.dtype).reshape(B, L, -1) * jax.nn.silu(ra)
    q = qb.reshape(B, L, SWA_KV_HEADS, SWA_GROUP, SWA_HD)
    k = kb.reshape(B, L, SWA_KV_HEADS, SWA_HD)
    v = vb.reshape(B, L, SWA_KV_HEADS, SWA_HD)
    if k_cache is None:
        o_b = swa_prompt(q, k, v, sinks)
        keep = min(WINDOW, L)
        k_new, v_new = k[:, -keep:], v[:, -keep:]
    else:
        kf = jnp.concatenate([k_cache.astype(k.dtype), k], axis=1)
        vf = jnp.concatenate([v_cache.astype(v.dtype), v], axis=1)
        o_b = sink_attention(q, kf, vf, sinks, None).reshape(B, L, SWA_HEADS * SWA_HD)
        keep = k_cache.shape[1]
        k_new, v_new = kf[:, -keep:], vf[:, -keep:]
    merged = jax.nn.sigmoid(ga) * o_a + jax.nn.sigmoid(gb) * o_b
    h = h + merged @ w_out
    h = h + 0.5 * swiglu(rmsnorm(h, g_ffn2), w2_up, w2_down)
    y = h + jax.nn.sigmoid(rmsnorm(h, g_ple) @ w_ple_gate) * (pe @ w_ple)
    return y, k_new, v_new, s_new.astype(s0.dtype)

def setup_inputs(seed: int = 0) -> dict:
    key = jax.random.key(seed)
    ks = jax.random.split(key, 32)
    nrm = jax.random.normal
    D = D_MODEL
    win = min(WINDOW, PAST_LEN)

    def gain(k, width):
        return 1.0 + 0.02 * nrm(k, (DEPTH, width), jnp.float32)

    return {
        'x_prompt': nrm(ks[0], (BATCH, SEQ, D), jnp.float32),
        'x_sample': nrm(ks[1], (DEC_BATCH, DEC_SEQ, D), jnp.float32),
        'p_prompt': nrm(ks[2], (DEPTH, BATCH, SEQ, PLE_DIM), jnp.float32),
        'p_sample': nrm(ks[3], (DEPTH, DEC_BATCH, DEC_SEQ, PLE_DIM), jnp.float32),
        'cache_swa_k': nrm(ks[4], (DEPTH, DEC_BATCH, win, SWA_KV_HEADS, SWA_HD), jnp.float32),
        'cache_swa_v': nrm(ks[5], (DEPTH, DEC_BATCH, win, SWA_KV_HEADS, SWA_HD), jnp.float32),
        'state_gla': 0.5 * nrm(ks[6], (DEPTH, DEC_BATCH, GLA_HEADS, GLA_DK, GLA_DV), jnp.float32),
        'g_ffn1': gain(ks[7], D),
        'w_ffn1_up': nrm(ks[8], (DEPTH, D, 2 * D_FF), jnp.float32) * D ** -0.5,
        'w_ffn1_down': nrm(ks[9], (DEPTH, D_FF, D), jnp.float32) * D_FF ** -0.5,
        'g_mix': gain(ks[10], D),
        'w_in': nrm(ks[11], (DEPTH, D, D_IN), jnp.float32) * D ** -0.5,
        'w_gla_a2': nrm(ks[12], (DEPTH, GLA_RANK, GLA_HEADS * GLA_DK), jnp.float32) * GLA_RANK ** -0.5,
        'b_gla_a': 0.01 * nrm(ks[13], (DEPTH, GLA_HEADS * GLA_DK), jnp.float32),
        'g_gla': gain(ks[14], GLA_HEADS * GLA_DV),
        'swa_sinks': 0.5 * nrm(ks[15], (DEPTH, SWA_HEADS), jnp.float32),
        'w_out': nrm(ks[16], (DEPTH, D, D), jnp.float32) * D ** -0.5,
        'g_ffn2': gain(ks[17], D),
        'w_ffn2_up': nrm(ks[18], (DEPTH, D, 2 * D_FF), jnp.float32) * D ** -0.5,
        'w_ffn2_down': nrm(ks[19], (DEPTH, D_FF, D), jnp.float32) * D_FF ** -0.5,
        'g_ple': gain(ks[20], D),
        'w_ple_gate': nrm(ks[21], (DEPTH, D, D), jnp.float32) * D ** -0.5,
        'w_ple': nrm(ks[22], (DEPTH, PLE_DIM, D), jnp.float32) * PLE_DIM ** -0.5,
        'g_final': 1.0 + 0.02 * nrm(ks[23], (D,), jnp.float32),
    }

def reference(x_prompt, x_sample, p_prompt, p_sample, cache_swa_k, cache_swa_v, state_gla,
              g_ffn1, w_ffn1_up, w_ffn1_down, g_mix, w_in, w_gla_a2, b_gla_a, g_gla, swa_sinks,
              w_out, g_ffn2, w_ffn2_up, w_ffn2_down, g_ple, w_ple_gate, w_ple, g_final):
    xp, xs = x_prompt, x_sample
    s0_prompt = jnp.zeros((x_prompt.shape[0], GLA_HEADS, GLA_DK, GLA_DV), jnp.float32)
    pk, pv, ps, sk, sv, ss = [], [], [], [], [], []
    for i in range(DEPTH):
        w = (g_ffn1[i], w_ffn1_up[i], w_ffn1_down[i], g_mix[i], w_in[i], w_gla_a2[i], b_gla_a[i],
             g_gla[i], swa_sinks[i], w_out[i], g_ffn2[i], w_ffn2_up[i], w_ffn2_down[i],
             g_ple[i], w_ple_gate[i], w_ple[i])
        xp, k1, v1, s1 = layer(xp, p_prompt[i], s0_prompt, None, None, *w)
        xs, k2, v2, s2 = layer(xs, p_sample[i], state_gla[i], cache_swa_k[i], cache_swa_v[i], *w)
        pk.append(k1); pv.append(v1); ps.append(s1)
        sk.append(k2); sv.append(v2); ss.append(s2)
    y_prompt = rmsnorm(xp, g_final)
    y_sample = rmsnorm(xs, g_final)
    return (y_prompt, y_sample, jnp.stack(pk), jnp.stack(pv), jnp.stack(ps),
            jnp.stack(sk), jnp.stack(sv), jnp.stack(ss))


_drawn_inputs = setup_inputs


def setup_inputs(seed=0):
    import zlib

    import numpy as np

    out = dict(_drawn_inputs(seed))
    spreads = {}
    factors = {'g_ffn1': 4.087,
     'b_gla_a': 8.0,
     'g_gla': 29.828,
     'swa_sinks': 64.0,
     'g_ffn2': 5.87,
     'g_ple': 64.0,
     'g_final': 8.417}
    for name, (base, spread) in spreads.items():
        noise = np.random.default_rng([zlib.crc32(name.encode()), seed]).standard_normal(out[name].shape)
        drawn = base * np.exp(spread * noise) if base else spread * noise
        out[name] = __import__('jax').numpy.asarray(drawn.astype(out[name].dtype))
    for name, factor in factors.items():
        out[name] = (out[name] * factor).astype(out[name].dtype)
    return out
```

```python
from contextlib import ExitStack

import concourse.bass as bass
from concourse import mybir

P = 128
D = 1024
DEPTH = 2
DFF = 2816
T_PROMPT, T_SAMPLE = 256, 64
T = T_PROMPT + T_SAMPLE
KD_ = D // P
FF = DFF // P
COLS = 256
EPS = 1e-6
HEADS, DK, DV, RANK, TAU = 4, 128, 256, 16, 16.0
KVH, HD, CACHE = 4, 64, 128

C_GA, C_GB, C_QA, C_KA, C_VA, C_RA, C_LR, C_QB, C_KB, C_VB = (
    0, 1024, 2048, 2560, 3072, 4096, 5120, 5136, 6160, 6416)
MIX = ([("ka", C_KA), ("rank", C_LR), ("ka", C_KA + COLS)] + [("qa", C_QA + COLS * i) for i in range(2)]
       + [("va", C_VA + COLS * i) for i in range(4)] + [("kb", C_KB), ("vb", C_VB)]
       + [("qb", C_QB + COLS * i) for i in range(4)] + [("ga", C_GA + COLS * i) for i in range(4)]
       + [("ra", C_RA + COLS * i) for i in range(4)] + [("gb", C_GB + COLS * i) for i in range(4)])
KIND = [k for k, _ in MIX]
FIRST = {k: KIND.index(k) for k in set(KIND)}
NTH = [KIND[:w].count(k) for w, k in enumerate(KIND)]
SET = [sum(k != "rank" for k in KIND[:w]) % 2 for w in range(len(KIND))]

PAIRS = FF // 2
PARTS = [(0, 6), (6, 6), (12, 5), (17, 5)]
U1 = 0
D1 = U1 + 2 * PAIRS
W_MIX = D1 + 4 * len(PARTS)
W_OUT = W_MIX + len(MIX)
U2 = W_OUT + 4
D2 = U2 + 2 * PAIRS
W_PLE = D2 + 4 * len(PARTS)
W_PG = W_PLE + 1
UNITS = W_PG + 4
RAW_SLOTS, SPLIT_SLOTS = 4, 2
assert DEPTH == 2
assert UNITS % RAW_SLOTS == 0 and UNITS % SPLIT_SLOTS == 0


def kept_by(w):
    return sum(k in ("ka", "qa", "qb", "ga", "ra", "gb") for k in KIND[:w + 1])


def unit_size(v):
    for down in (D1, D2):
        if down <= v < down + 4 * len(PARTS):
            return PARTS[(v - down) % len(PARTS)][1] * COLS
    return KD_ * P if v == W_MIX + FIRST["rank"] else 2048


PIECES = ((P, 0, P, 0), (P, P, 320, 1), (64, 320, 512, 2))
HALVES = [64, 32, 16, 8, 4, 2, 1]
N_CONSTS = 8 + 3 + 2 * (2 * len(HALVES) - 1)
G_FFN1, G_MIX, G_FFN2, G_PLE, G_GLA, B_DECAY, VECS = 0, 8, 16, 24, 32, 40, 44


class Event:

    def __init__(self, sem, per_layer, start=0):
        self.sem, self.per_layer, self.start = sem, per_layer, start

    def __call__(self, layer, n):
        return self.sem, layer * self.per_layer + (n + self.start)


def trunk_kernel(nc, xT, peT, kcT, vc, s0, vecs, g_final, sinks,
                 w_up1, w_down1, w_in, w_a2, w_out, w_up2, w_down2, w_pg, w_ple,
                 yT, pk, pv_out, pstate, sk, sv, sstate):
    fp32, f32r, bf16, u16 = mybir.dt.float32, mybir.dt.float32r, mybir.dt.bfloat16, mybir.dt.uint16
    ALU, ACT, AX = mybir.AluOpType, mybir.ActivationFunctionType, mybir.AxisListType

    up1 = w_up1.rearrange("l (k p) c -> l p k c", p=P)
    up2 = w_up2.rearrange("l (k p) c -> l p k c", p=P)
    down1 = w_down1.rearrange("l (k p) c -> l p k c", p=P)
    down2 = w_down2.rearrange("l (k p) c -> l p k c", p=P)
    win = w_in.rearrange("l (k p) c -> l p k c", p=P)
    wout = w_out.rearrange("l (k p) c -> l p k c", p=P)
    wpg = w_pg.rearrange("l (k p) c -> l p k c", p=P)
    wple = w_ple.rearrange("l (k p) c -> l p k c", p=P)

    ctx = ExitStack()
    with ctx:
        def sb(name, shape, dt=fp32):
            return ctx.enter_context(nc.sbuf_tensor(name, shape, dt))

        raw = [sb(f"raw{i}", [P, 2048]) for i in range(RAW_SLOTS)]
        w_hi = [sb(f"w_hi{i}", [P, 2048], f32r) for i in range(SPLIT_SLOTS)]
        w_lo = [sb(f"w_lo{i}", [P, 2048], f32r) for i in range(SPLIT_SLOTS)]
        x = sb("x", [P, KD_, T])
        u_hi = sb("u_hi", [P, KD_ * T + 64], f32r)
        u_lo = sb("u_lo", [P, KD_ * T + 64], f32r)
        sq_acc = sb("sq_acc", [P, 2, T])
        sq = sb("sq", [P, 2, T])
        sq_sum = sb("sq_sum", [P, T + 64])
        scale = sb("scale", [P, T])
        tok_scale = sb("tok_scale", [P, 3])
        wide = sb("wide", [P, 2, T])
        ones = sb("ones", [P, P])
        ident = sb("ident", [P, P])
        masks = sb("masks", [P, len(HALVES), 160], bf16)
        diag = sb("diag", [P, T], bf16)
        sT = sb("sT", [P, HEADS, T])
        vec = sb("vec", [P, (DEPTH + 1) * VECS])
        gfin = sb("gfin", [P, KD_])
        nsink = sb("nsink", [P, DEPTH * 16])
        eps = sb("eps", [P, 1])
        row_max = sb("row_max_t", [P, 2, 3])
        shift = sb("shift_t", [P, 2, 3])
        sink_d = sb("sink_d", [P, 2, 3])
        sums = sb("sums_t", [P, 2, 3])
        den = sb("den_t", [P, 2, 3])
        last_decay = sb("last_decay", [P, HEADS, 2])

        with ExitStack() as ffn:
            def fb(name, shape, dt=fp32):
                return ffn.enter_context(nc.sbuf_tensor(name, shape, dt))
            h_hi = fb("h_hi", [P, FF, T], f32r)
            h_lo = fb("h_lo", [P, FF, T], f32r)
            gate = fb("gate", [P, 2, T])
            h_wide = fb("h_wide", [P, 2, T])
            pe_raw = fb("pe_raw", [P, 2, T])
            pe_hi = fb("pe_hi", [P, 2, T], f32r)
            pe_lo = fb("pe_lo", [P, 2, T], f32r)
            ple = fb("ple", [P, KD_, T])
        with ExitStack() as late:
            merged_hi = late.enter_context(nc.sbuf_tensor("merged_hi", [P, KD_ * T + 64], f32r))
            merged_lo = late.enter_context(nc.sbuf_tensor("merged_lo", [P, KD_ * T], f32r))
        mix = ExitStack()
        with mix:
            def mb(name, shape, dt=fp32):
                return mix.enter_context(nc.sbuf_tensor(name, shape, dt))
            qk = mb("qk", [P, 2 * HEADS * T + 64])
            vg = mb("vg", [P, 3 * HEADS * DV])
            bo = mb("bo", [P, KD_ * T])
            span = mb("span", [P, HEADS * T])
            wk = mb("wk", [P, HEADS * T + 64 + 3 * 512])
            s_prompt = mb("s_prompt", [P, HEADS, DV])
            s_sample = mb("s_sample", [P, HEADS, DV])
            qs = mb("qs", [P, KD_, T])
            kd = mb("kd", [P, KVH, T + CACHE])
            vs = mb("vs", [P, 3, KVH * HD])
            vs_shift = mb("vs_shift", [P, 2, KVH * HD])
            vcache = mb("vcache", [P, KVH * HD])
        q_gla = qk[:, 0:HEADS * T].rearrange("p (h t) -> p h t", h=HEADS)
        k_gla = qk[:, HEADS * T:2 * HEADS * T].rearrange("p (h t) -> p h t", h=HEADS)
        k_flat = qk[:, HEADS * T:2 * HEADS * T + 64]
        gate_a = qk[:, 0:KD_ * T].rearrange("p (c t) -> p c t", c=KD_)
        cum = bo[:, 0:HEADS * T].rearrange("p (h t) -> p h t", h=HEADS)
        o_gla = bo[:, :].rearrange("p (c t) -> p c t", c=KD_)
        span_h = span[:, :].rearrange("p (h t) -> p h t", h=HEADS)
        pair_flat = wk[:, 0:HEADS * T + 64]
        pair = wk[:, 0:HEADS * T].rearrange("p (h t) -> p h t", h=HEADS)
        k_rows = wk[:, HEADS * T + 64:].rearrange("p (t c) -> p t c", t=3)
        rank = wk[0:RANK, HEADS * T + 64:HEADS * T + 64 + T]
        wa2 = wk[0:RANK, HEADS * T + 64 + T:HEADS * T + 64 + T + HEADS * DK]
        probs = [t[:, 0:1024].rearrange("p (e c) -> p e c", e=2) for t in (wk, span)]
        probs_t = wk[:, 1024:2048].rearrange("p (e c) -> p e c", e=2)
        v_gla = vg[:, :].rearrange("p (t c) -> p t c", t=3)
        gate_b = vg[:, 0:KD_ * T].rearrange("p (c t) -> p c t", c=KD_)

        sets = [ctx.enter_context(nc.psum_tensor(f"set{i}", [P, 2, 512], fp32)) for i in range(2)]
        aux = ctx.enter_context(nc.psum_tensor("aux", [P, 4, 512], fp32))

        def gain_of(layer, n):
            return vec[:, bass.ds(layer * VECS + n, 1)]

        ple_place = (sets[0], aux[:, 2:4, :], aux[:, 0:2, :], sets[1])

        def ev(name, per_layer, start=0):
            return Event(ctx.enter_context(nc.semaphore(name)), per_layer, start)

        raw_loaded = [ev(f"raw_loaded{i}", 16 * UNITS // RAW_SLOTS) for i in range(RAW_SLOTS)]
        high_done = ev("high_done", UNITS)
        split_done = ev("split_done", UNITS, RAW_SLOTS)
        products_done = ev("products_done", UNITS, SPLIT_SLOTS)
        x_ready = ev("x_ready", 16, 4)
        sq_ready = ev("sq_ready", 16, 4)
        acc_ready = ev("acc_ready", 12, 3)
        sum_ready = ev("sum_ready", 4, 1)
        norm_sum = ev("norm_sum", 4)
        norm_root = ev("norm_root", 4)
        norm_scale = ev("norm_scale", 4)
        token_root = ev("token_root", 1)
        token_scale = ev("token_scale", 1)
        u_high = ev("u_high", 32)
        u_ready = ev("u_ready", 32)
        merged_wide = ev("merged_wide", 4)
        merged_high = ev("merged_high", 4)
        merged_ready = ev("merged_ready", 4)
        gate_in = ev("gate_in", 2 * PAIRS)
        gate_scaled = ev("gate_scaled", 2 * PAIRS)
        silu_done = ev("silu_done", 2 * PAIRS)
        h_full = ev("h_full", 2 * PAIRS, 1)
        h_high = ev("h_high", 2 * PAIRS)
        h_ready = ev("h_ready", 2 * PAIRS, 1)
        pe_loaded = ev("pe_loaded", 16)
        pe_high = ev("pe_high", 1)
        pe_ready = ev("pe_ready", 1)
        ple_done = ev("ple_done", 3)
        ple_kept = ev("ple_kept", 4)
        pg_in = ev("pg_in", 4)
        pg_gate = ev("pg_gate", 4)
        pg_prod = ev("pg_prod", 4)
        mix_loaded = ev("mix_loaded", 16 * 5)
        stored = ev("stored", 16 * 8)
        mix_kept = ev("mix_kept", kept_by(len(MIX) - 1))
        values_kept = ev("values_kept", 5)
        gate_tanh = ev("gate_tanh", 4)
        gate_b_tanh = ev("gate_b_tanh", 4)
        kb_kept = ev("kb_kept", 4)
        ra_read = ev("ra_read", 4)
        ra_gate = ev("ra_gate", 4)
        ra_tanh = ev("ra_tanh", 4)
        oa_gated = ev("oa_gated", 4)
        ob_gated = ev("ob_gated", 4)
        rank_kept = ev("rank_kept", 1)
        pads_cleared = ev("pads_cleared", 2)
        v_part = ev("v_part", 10)
        logits = ev("logits", 1)
        logit_full = ev("logit_full", HEADS)
        logit_floor = ev("logit_floor", 1)
        logit_abs = ev("logit_abs", 1)
        logit_exp = ev("logit_exp", 1)
        logit_log = ev("logit_log", 1)
        cum_done = ev("cum_done", 3 * HEADS)
        diag_done = ev("diag_done", 1)
        diag_kept = ev("diag_kept", 1)
        span_done = ev("span_done", 2 * len(HALVES))
        span_exp = ev("span_exp", len(HALVES))
        pair_done = ev("pair_done", 2 * len(HALVES))
        level_done = ev("level_done", len(HALVES))
        level_kept = ev("level_kept", 2 * len(HALVES))
        carry_exp = ev("carry_exp", 1)
        q_carried = ev("q_carried", 1)
        key_span = ev("key_span", 2)
        key_exp = ev("key_exp", 1)
        k_carried = ev("k_carried", 1)
        last_exp = ev("last_exp", 1)
        keys_turned = ev("keys_turned", 1)
        keys_kept = ev("keys_kept", 1)
        keys_tail = ev("keys_tail", 1)
        state_sum = ev("state_sum", 3)
        state_first = ev("state_first", 1)
        state_new = ev("state_new", 2 * HEADS)
        gla_out = ev("gla_out", 2)
        gla_kept = ev("gla_kept", 2)
        gla_sq = ev("gla_sq", 2)
        gla_sq_sum = ev("gla_sq_sum", 2)
        gla_sum = ev("gla_sum", 2)
        gla_root = ev("gla_root", 2)
        gla_scale = ev("gla_scale", 2)
        gla_norm = ev("gla_norm", 8)
        v_shifted = ev("v_shifted", 3)
        band_closed = ev("band_closed", 1)
        scores_done = ev("scores_done", 8)
        max_done = ev("max_done", 24)
        shift_done = ev("shift_done", 8)
        sink_diff = ev("sink_diff", 8)
        probs_done = ev("probs_done", 48)
        sink_exp = ev("sink_exp", 8)
        den_done = ev("den_done", 8)
        recip_done = ev("recip_done", 8)
        scaled = ev("scaled", 24)
        turned = ev("turned", 8)
        turned_kept = ev("turned_kept", 32)
        
        heads_out = ev("heads_out", 8)
        heads_kept = ev("heads_kept", 8)
        consts = ev("consts", 0)
        x_loaded = ev("x_loaded", 0)
        loaded = ev("loaded", 0)
        vec_init = ev("vec_init", 0)
        y_done = ev("y_done", 0)
        y_stored = ev("y_stored", 0)
        final_sum = ev("final_sum", 0)
        final_root = ev("final_root", 0)
        final_scale = ev("final_scale", 0)

        block = ctx.enter_context(nc.Block())

        @block.sync
        def _(sp):
            def load(layer, v, src, n_k, cols, extra=0, ahead=None):
                slot = v % RAW_SLOTS
                sp.wait_ge(*split_done(layer, v + extra - (RAW_SLOTS - 1)))
                if ahead is not None:
                    ahead(layer)
                dst = raw[slot][:, 0:n_k * cols].rearrange("p (k c) -> p k c", k=n_k)
                sp.dma_start(dst, src).then_inc(raw_loaded[slot].sem, 16)

            def load_up(layer, first, w, loaded):
                with sp.Fori(0, PAIRS // 2) as i:
                    for j in range(loaded, loaded + 4):
                        c0 = DFF * (j % 2) + COLS * (j // 2)
                        load(layer, first + j, w[layer, :, :, bass.ds(i * (2 * COLS) + c0, COLS)], KD_, COLS, i * 4)
                for j in range(loaded, 2):
                    c0 = DFF * j + COLS * (PAIRS - 1)
                    load(layer, first + 2 * (PAIRS - 1) + j, w[layer, :, :, c0:c0 + COLS], KD_, COLS)

            def load_down(layer, first, w):
                with sp.Fori(0, 4) as g:
                    for j, (k0, n) in enumerate(PARTS):
                        load(layer, first + j, w[layer, :, k0:k0 + n, bass.ds(g * COLS, COLS)], n, COLS, g * 4)

            def copy(dst, src, event, *waits):
                for wait in waits:
                    sp.wait_ge(*wait)
                sp.dma_start(dst, src).then_inc(event.sem, 16)

            def store_keys(layer):
                copy(pk[layer], kd[0:HD, :, T_PROMPT - P:T_PROMPT], stored, kb_kept(layer, 4), mix_loaded(layer, 80))
                copy(sk[layer, :, :, 0:CACHE - T_SAMPLE], kd[0:HD, :, T + T_SAMPLE:], stored)
                copy(sk[layer, :, :, CACHE - T_SAMPLE:], kd[0:HD, :, T_PROMPT:T], stored)

            def between(layer, w):
                if w == 5:
                    copy(wa2, w_a2[layer], mix_loaded, products_done(layer, W_MIX))
                    copy(kd[0:HD, :, T:], kcT[layer], mix_loaded)
                    copy(kd[HD:P, :, T:], kcT[layer], mix_loaded)
                    copy(vcache[:, :], vc[layer], mix_loaded)
                    copy(s_sample[:, :, :], s0[layer].rearrange("h k v -> k h v"), mix_loaded)
                if w == FIRST["vb"] + 7:
                    copy(pv_out[layer], vs[:, 1, :], stored, values_kept(layer, 5))
                    copy(sv[layer, 0:CACHE - T_SAMPLE, :], vcache[T_SAMPLE:, :], stored)
                    copy(sv[layer, CACHE - T_SAMPLE:, :], vs[0:T_SAMPLE, 2, :], stored)
                if w == 24:
                    copy(pstate[layer].rearrange("h k v -> k h v"), s_prompt[:, :, :], stored, state_new(layer, 2 * HEADS))
                    copy(sstate[layer].rearrange("h k v -> k h v"), s_sample[:, :, :], stored)

            load(0, U1, up1[0, :, :, 0:COLS], KD_, COLS)
            sp.dma_start(x[:, :, :], xT).then_inc(x_loaded.sem, 16)
            with sp.Fori(0, DEPTH) as layer:
                load_up(layer, U1, up1, 1)
                load_down(layer, D1, down1)
                for w, (kind, c0) in enumerate(MIX):
                    cols = P if kind == "rank" else COLS
                    load(layer, W_MIX + w, win[layer, :, :, c0:c0 + cols], KD_, cols, ahead=store_keys if c0 == 0 else None)
                    between(layer, w)
                for j in range(4):
                    load(layer, W_OUT + j, wout[layer, :, :, j * COLS:(j + 1) * COLS], KD_, COLS)
                load_up(layer, U2, up2, 0)
                copy(pe_raw[:, :, :], peT[layer], pe_loaded, stored(layer, 128))
                load_down(layer, D2, down2)
                load(layer, W_PLE, wple[layer], 2, D)
                for j in range(4):
                    load(layer, W_PG + j, wpg[layer, :, :, j * COLS:(j + 1) * COLS], KD_, COLS)
                load(layer, UNITS, up1[layer * -1 + (DEPTH - 1), :, :, 0:COLS], KD_, COLS)
            for j in range(4):
                sp.wait_ge(y_done.sem, 2 * (j + 1))
                sp.dma_start(yT[:, 2 * j:2 * j + 2, :], x[:, 2 * j:2 * j + 2, :]).then_inc(y_stored.sem, 16)
            sp.wait_ge(y_stored.sem, 64)

        @block.gpsimd
        def _(pool):
            pool.dma_start(gfin[:, :], g_final).then_inc(loaded.sem, 16)
            pool.dma_start(nsink[:, :], sinks.rearrange("(o l) h -> o (l h)", o=1).broadcast_to([P, DEPTH * 16])).then_inc(loaded.sem, 16)
            count = [0]

            def const(ins):
                count[0] += 1
                ins.then_inc(consts.sem, 1)

            def after_const():
                pool.wait_ge(consts.sem, count[0])

            const(pool.memset(ones[:, :], 1.0))
            const(pool.memset(ident[:, :], 0.0))
            const(pool.memset(eps[:, :], EPS))
            const(pool.memset(masks[:, :, :], 1.0))
            const(pool.memset(diag[:, :], 0.0))
            const(pool.memset(sT[:, :, :], 0.0))
            const(pool.memset(row_max[:, :, :], 0.0))
            const(pool.memset(sums[:, :, :], 1.0))
            after_const()
            const(pool.affine_select(out=ident[:, :], in_=ident[:, :], compare_op=ALU.not_equal, fill=1.0,
                                     base=0, pattern=[[-1, P]], channel_multiplier=1))
            dg = diag[:, 0:2 * P].rearrange("p (t i) -> p t i", t=2)
            const(pool.affine_select(out=dg, in_=dg, compare_op=ALU.not_equal, fill=1.0,
                                     base=0, pattern=[[0, 2], [-1, P]], channel_multiplier=1))
            dg = diag[:, 2 * P:T]
            const(pool.affine_select(out=dg, in_=dg, compare_op=ALU.not_equal, fill=1.0,
                                     base=0, pattern=[[-1, T - 2 * P]], channel_multiplier=1))
            for n, half in enumerate(HALVES):
                for at, tiles, width in ((0, 2, 64), (128, 1, 32)):
                    if half > width:
                        continue
                    m = masks[:, n, at:at + tiles * width].rearrange("p (t b i) -> p t b i", t=tiles, i=half)
                    blocks = width // half
                    const(pool.affine_select(out=m, in_=m, compare_op=ALU.is_ge, fill=0.0, base=0,
                                             pattern=[[0, tiles], [-2 * half, blocks], [0, half]], channel_multiplier=1))
                    after_const()
                    const(pool.affine_select(out=m, in_=m, compare_op=ALU.is_ge, fill=0.0, base=half - 1,
                                             pattern=[[0, tiles], [2 * half, blocks], [0, half]], channel_multiplier=-1))
            assert count[0] == N_CONSTS, count[0]
            with pool.Fori(0, DEPTH) as layer:
                for i in range(4):
                    pool.wait_ge(*gla_norm(layer, 8))
                    pool.wait_ge(*ra_gate(layer, i + 1))
                    o = o_gla[:, 2 * i:2 * i + 2, :]
                    pool.tensor_tensor(o, o, gate_a[:, 2 * i:2 * i + 2, :], ALU.mult).then_inc(oa_gated.sem, 1)

        @block.scalar
        def _(act):
            def high(layer, v, extra=0):
                n = unit_size(v)
                act.wait_ge(*raw_loaded[v % RAW_SLOTS](layer, 16 * (v // RAW_SLOTS + 1) + extra * (16 // RAW_SLOTS)))
                act.wait_ge(*products_done(layer, v + extra - (SPLIT_SLOTS - 1)))
                act.activation(w_hi[v % SPLIT_SLOTS][:, 0:n], raw[v % RAW_SLOTS][:, 0:n], ACT.Copy).then_inc(high_done.sem, 1)

            def square(layer, n, g):
                act.wait_ge(*x_ready(layer, 4 * (n - 1) + g + 1))
                if g == 0:
                    act.wait_ge(*sum_ready(layer, n - 1))
                elif g >= 2:
                    act.wait_ge(*acc_ready(layer, 3 * (n - 1) + g - 1))
                dst = sq_acc if g == 0 else sq
                act.activation(dst[:, :, :], x[:, 2 * g:2 * g + 2, :], ACT.Square).then_inc(sq_ready.sem, 1)

            def u_upper(layer, n, g):
                gain = [G_FFN1, G_MIX, G_FFN2, G_PLE, VECS + G_FFN1][n]
                act.wait_ge(*x_ready(layer, 4 * (n - 1) + g + 1))
                for c in (2 * g, 2 * g + 1):
                    act.activation(u_hi[:, c * T:(c + 1) * T], x[:, c, :], ACT.Copy,
                                   scale=gain_of(layer, gain + c)).then_inc(u_high.sem, 1)

            def norm(layer, n):
                act.wait_ge(*norm_sum(layer, n + 1))
                act.activation(scale[:, :], aux[:, 0, 0:T], ACT.Sqrt, scale=1.0 / D, bias=eps[:, 0:1]).then_inc(norm_root.sem, 1)
                if n == 1:
                    act.activation(tok_scale[:, :], aux[:, 1, 0:3], ACT.Sqrt, scale=1.0 / D, bias=eps[:, 0:1]).then_inc(token_root.sem, 1)

            def silu(layer, n):
                act.wait_ge(*gate_in(layer, n + 1))
                act.activation(gate[:, :, :], gate[:, :, :], ACT.Silu).then_inc(silu_done.sem, 1)

            def hidden_high(layer, n, pair_index):
                act.wait_ge(*h_full(layer, n + 1))
                act.activation(h_hi[:, bass.ds(pair_index * 2, 2), :], h_wide[:, :, :], ACT.Copy).then_inc(h_high.sem, 1)

            def ffn(layer, first, f):
                with act.Fori(0, (PAIRS - 1) // 2) as i:
                    for j in range(2):
                        v = first + 2 * (j + 1)
                        high(layer, v, extra=i * 4)
                        silu(layer, f * PAIRS + i * 2 + j)
                        high(layer, v + 1, extra=i * 4)
                        hidden_high(layer, f * PAIRS + i * 2 + j, i * 2 + j)
                down = first + 2 * PAIRS
                high(layer, down)
                silu(layer, f * PAIRS + PAIRS - 1)
                high(layer, down + 1)
                hidden_high(layer, f * PAIRS + PAIRS - 1, PAIRS - 1)
                high(layer, down + 2)
                high(layer, down + 3)
                n = 1 if f == 0 else 3
                for g in range(1, 4):
                    high(layer, down + 4 * g)
                    high(layer, down + 4 * g + 1)
                    u_upper(layer, n, g - 1)
                    square(layer, n, g - 1)
                    high(layer, down + 4 * g + 2)
                    high(layer, down + 4 * g + 3)

            def keep(layer, w):
                kind = KIND[w]
                i = NTH[w]
                src = sets[SET[w]]
                if kind in ("va", "vb"):
                    act.wait_ge(*token_scale(layer, 1))
                    act.wait_ge(*products_done(layer, W_MIX + w + 1))
                    dst = v_gla[:, :, i * COLS:(i + 1) * COLS] if kind == "va" else vs[:, :, :]
                    for t in range(3):
                        tile = src[:, t // 2, (t % 2) * COLS:(t % 2 + 1) * COLS]
                        act.activation(dst[:, t, :], tile, ACT.Copy,
                                       scale=tok_scale[:, t:t + 1]).then_inc((v_part if t < 2 else values_kept).sem, 1)
                elif kind == "ga":
                    act.wait_ge(*mix_kept(layer, kept_by(w)))
                    g = gate_a[:, 2 * i:2 * i + 2, :]
                    act.activation(g, g, ACT.Tanh, scale=0.5).then_inc(gate_tanh.sem, 1)
                elif kind == "ra":
                    act.wait_ge(*mix_kept(layer, kept_by(w)))
                    if i == 0:
                        act.wait_ge(*gla_norm(layer, 8))
                    else:
                        act.wait_ge(*ra_gate(layer, i))
                    act.activation(wide[:, :, :], sq[:, :, :], ACT.Tanh, scale=2.0).then_inc(ra_tanh.sem, 1)
                elif kind == "gb":
                    act.wait_ge(*mix_kept(layer, kept_by(w)))
                    g = gate_b[:, 2 * i:2 * i + 2, :]
                    act.activation(g, g, ACT.Tanh, scale=0.5).then_inc(gate_b_tanh.sem, 1)

            def merged_upper(layer, i):
                act.wait_ge(*merged_wide(layer, i + 1))
                act.activation(merged_hi[:, 2 * i * T:2 * (i + 1) * T], wide[:, :, :].rearrange("p c t -> p (c t)"),
                               ACT.Copy).then_inc(merged_high.sem, 1)

            def heads_keep(layer, c):
                act.wait_ge(*heads_out(layer, c + 1))
                act.activation(qs[:, c, :], aux[:, 2, 0:T], ACT.Copy).then_inc(heads_kept.sem, 1)

            def level_exp(layer, i):
                act.wait_ge(*span_done(layer, 2 * i + 2))
                n = T_PROMPT if HALVES[i] == 64 else T
                act.activation(span_h[:, :, 0:n], span_h[:, :, 0:n], ACT.Exp, scale=1.0 / TAU).then_inc(span_exp.sem, 1)

            def gla_square(layer, r):
                act.wait_ge(*gla_kept(layer, r + 1))
                act.activation(span_h[:, :, :], o_gla[:, 4 * r:4 * r + 4, :], ACT.Square).then_inc(gla_sq.sem, 1)

            def attend(layer, w):
                if w == 2:
                    act.wait_ge(*logit_full(layer, HEADS))
                    act.activation(pair[:, :, :], span_h[:, :, :], ACT.Abs).then_inc(logit_abs.sem, 1)
                    act.wait_ge(*logit_abs(layer, 1))
                    act.activation(pair[:, :, :], pair[:, :, :], ACT.Exp, scale=-1.0).then_inc(logit_exp.sem, 1)
                if w == 3:
                    act.wait_ge(*logit_exp(layer, 1))
                    act.activation(pair[:, :, :], pair[:, :, :], ACT.Ln, bias=1.0).then_inc(logit_log.sem, 1)
                if w == 4:
                    level_exp(layer, 0)
                if w == 5:
                    level_exp(layer, 1)
                if 7 <= w < 7 + len(HALVES) - 2:
                    level_exp(layer, w - 5)
                if w == 12:
                    act.wait_ge(*pair_done(layer, 2 * len(HALVES)))
                    act.activation(span_h[:, :, P:T], cum[:, :, P:T], ACT.Exp, scale=1.0 / TAU).then_inc(carry_exp.sem, 1)
                if w == 13:
                    act.wait_ge(*key_span(layer, 2))
                    act.activation(span[:, :], span[:, :], ACT.Exp, scale=1.0 / TAU).then_inc(key_exp.sem, 1)
                    act.activation(last_decay[:, :, :], cum[:, :, 255:T:64], ACT.Exp, scale=1.0 / TAU).then_inc(last_exp.sem, 1)
                if w == 14:
                    act.wait_ge(*keys_turned(layer, 1))
                    act.activation(k_rows[:, 0:2, :], aux[:, 0:2, :], ACT.Copy).then_inc(keys_kept.sem, 1)
                    act.wait_ge(*state_sum(layer, 1))
                    act.activation(s_prompt[:, :, :], aux[:, 0:2, :].rearrange("p b (h v) -> p (b h) v", h=2), ACT.Copy).then_inc(state_first.sem, 1)
                if w in (15, 16):
                    r = w - 15
                    act.wait_ge(*gla_sum(layer, r + 1))
                    if r == 1:
                        act.wait_ge(*gla_norm(layer, 4))
                    act.activation(wide[:, :, :], aux[:, 2 * r:2 * r + 2, 0:T], ACT.Sqrt, scale=1.0 / DV, bias=eps[:, 0:1]).then_inc(gla_root.sem, 1)
                if 20 <= w:
                    heads_keep(layer, w - 20)
                if 18 <= w <= 25:
                    c = w - 18
                    act.wait_ge(*shift_done(layer, c + 1))
                    if c == 1:
                        act.wait_ge(*gla_sum(layer, 2))
                    if c > 1:
                        act.wait_ge(*turned(layer, c - 1))
                    if c > 0:
                        act.wait_ge(*recip_done(layer, c))
                    for e in range(2):
                        for hi, c0, c1, col in PIECES:
                            act.activation(probs[c % 2][0:hi, e, c0:c1], aux[0:hi, e, c0:c1], ACT.Exp, scale=HD ** -0.5,
                                           bias=shift[0:hi, e, col:col + 1], accum_out=sums[0:hi, e, col:col + 1]).then_inc(probs_done.sem, 1)
                    act.wait_ge(*sink_diff(layer, c + 1))
                    act.activation(sink_d[:, :, :], sink_d[:, :, :], ACT.Exp).then_inc(sink_exp.sem, 1)

            def probs_keep(layer, c):
                act.wait_ge(*turned(layer, c + 1))
                if c > 0:
                    act.wait_ge(*heads_out(layer, c))
                for e in range(2):
                    act.activation(probs_t[:, e, 0:320], aux[:, 2 + e, 0:320], ACT.Copy).then_inc(turned_kept.sem, 1)
                    act.activation(probs_t[0:64, e, 320:512], aux[0:64, 2 + e, 320:512], ACT.Copy).then_inc(turned_kept.sem, 1)

            act.dma_start(vec[:, 0:DEPTH * VECS].rearrange("p (l v) -> p l v", l=DEPTH), vecs.rearrange("l p v -> p l v")).then_inc(x_loaded.sem, 16)
            high(0, U1)
            act.wait_ge(x_loaded.sem, 32)
            u_upper(0, 0, 0)
            act.activation(sq_acc[:, :, :], x[:, 0:2, :], ACT.Square).then_inc(sq_ready.sem, 1)
            act.activation(sq[:, :, :], x[:, 2:4, :], ACT.Square).then_inc(sq_ready.sem, 1)
            u_upper(0, 0, 1)
            act.wait_ge(acc_ready.sem, 1)
            act.activation(sq[:, :, :], x[:, 4:6, :], ACT.Square).then_inc(sq_ready.sem, 1)
            u_upper(0, 0, 2)
            act.wait_ge(acc_ready.sem, 2)
            act.activation(sq[:, :, :], x[:, 6:8, :], ACT.Square).then_inc(sq_ready.sem, 1)
            with act.Fori(0, DEPTH) as layer:
                u_upper(layer, 0, 3)
                high(layer, U1 + 1)
                act.wait_ge(consts.sem, 3)
                norm(layer, 0)
                ffn(layer, U1, 0)
                high(layer, W_MIX)
                u_upper(layer, 1, 3)
                square(layer, 1, 3)
                for w in range(len(MIX)):
                    if w < 17:
                        if w in (15, 16):
                            gla_square(layer, w - 15)
                        if w >= 1:
                            keep(layer, w - 1)
                    high(layer, W_MIX + w + 1)
                    if w == 1:
                        norm(layer, 1)
                    attend(layer, w)
                    if w >= 17:
                        keep(layer, w - 1)
                    if w >= 19:
                        probs_keep(layer, w - 19)
                    if w >= 24:
                        merged_upper(layer, w - 24)
                keep(layer, len(MIX) - 1)
                heads_keep(layer, 7)
                high(layer, W_OUT + 1)
                merged_upper(layer, 3)
                for j in range(4):
                    if j < 3:
                        high(layer, W_OUT + j + 2)
                    u_upper(layer, 2, j)
                    square(layer, 2, j)
                high(layer, U2 + 1)
                norm(layer, 2)
                act.wait_ge(*stored(layer, 128))
                ffn(layer, U2, 1)
                act.wait_ge(*pe_loaded(layer, 16))
                act.activation(pe_hi[:, :, :], pe_raw[:, :, :], ACT.Copy).then_inc(pe_high.sem, 1)
                high(layer, W_PLE)
                u_upper(layer, 3, 3)
                square(layer, 3, 3)
                high(layer, W_PG)
                for c in range(4):
                    if c < 3:
                        act.wait_ge(*ple_done(layer, c + 1))
                    else:
                        act.wait_ge(*products_done(layer, W_PLE + 1))
                    src = ple_place[c]
                    act.activation(ple[:, 2 * c:2 * c + 2, :], src[:, :, 0:T], ACT.Copy).then_inc(ple_kept.sem, 1)
                high(layer, W_PG + 1)
                norm(layer, 3)
                for j in range(4):
                    if j < 3:
                        high(layer, W_PG + j + 2)
                    if j == 3:
                        act.wait_ge(*products_done(layer, UNITS))
                        u_upper(layer, 4, 0)
                    act.wait_ge(*pg_in(layer, j + 1))
                    act.activation(gate[:, :, :], gate[:, :, :], ACT.Sigmoid).then_inc(pg_gate.sem, 1)
                    if j == 3:
                        u_upper(layer, 4, 1)
                        u_upper(layer, 4, 2)
                    square(layer, 4, j)
            act.wait_ge(final_sum.sem, 1)
            act.activation(scale[:, :], aux[:, 0, 0:T], ACT.Sqrt, scale=1.0 / D, bias=eps[:, 0:1]).then_inc(final_root.sem, 1)

        @block.vector
        def _(dve):
            def low(layer, v, extra=0):
                dve.wait_ge(*high_done(layer, v + extra + 1))
                slot, n = v % SPLIT_SLOTS, unit_size(v)
                dve.tensor_tensor(w_lo[slot][:, 0:n], raw[v % RAW_SLOTS][:, 0:n],
                                  w_hi[slot][:, 0:n].bitcast(fp32), ALU.subtract).then_inc(split_done.sem, 1)

            def scale_of(n, parts=P):
                return scale[0:parts, :].rearrange("p (o t) -> p o t", o=1).broadcast_to([parts, n, T])

            def residual(layer, n, g, last_unit, factor):
                dve.wait_ge(*products_done(layer, last_unit + 1))
                xs = x[:, 2 * g:2 * g + 2, :]
                dve.scalar_tensor_tensor(out=xs, in0=sets[g % 2][:, :, 0:T], scalar=factor, in1=xs,
                                         op0=ALU.mult, op1=ALU.add).then_inc(x_ready.sem, 1)

            def u_lower(layer, n, g):
                gain = [G_FFN1, G_MIX, G_FFN2, G_PLE, VECS + G_FFN1][n]
                for c in (2 * g, 2 * g + 1):
                    dve.wait_ge(*u_high(layer, 8 * n + c + 1))
                    cols = slice(c * T, (c + 1) * T)
                    dve.scalar_tensor_tensor(out=u_lo[:, cols], in0=x[:, c, :], scalar=gain_of(layer, gain + c),
                                             in1=u_hi[:, cols].bitcast(fp32), op0=ALU.mult, op1=ALU.subtract).then_inc(u_ready.sem, 1)

            def add_squares(layer, n, g):
                dve.wait_ge(*sq_ready(layer, 4 * (n - 1) + g + 1))
                if g > 1:
                    dve.wait_ge(*acc_ready(layer, 3 * (n - 1) + g - 1))
                dve.tensor_tensor(sq_acc[:, :, :], sq_acc[:, :, :], sq[:, :, :], ALU.add).then_inc(acc_ready.sem, 1)
                if g == 3:
                    dve.wait_ge(*acc_ready(layer, 3 * n))
                    dve.wait_ge(*norm_sum(layer, n))
                    dve.tensor_tensor(sq_sum[:, 0:T], sq_acc[:, 0, :], sq_acc[:, 1, :], ALU.add).then_inc(sum_ready.sem, 1)

            def norm(layer, n):
                dve.wait_ge(*norm_root(layer, n + 1))
                dve.reciprocal(scale[:, :], scale[:, :]).then_inc(norm_scale.sem, 1)
                if n == 1:
                    dve.wait_ge(*token_root(layer, 1))
                    dve.reciprocal(tok_scale[:, :], tok_scale[:, :]).then_inc(token_scale.sem, 1)

            def gate_take(layer, f, n, up_unit, extra=0):
                dve.wait_ge(*norm_scale(layer, 2 * f + 1))
                dve.wait_ge(*h_full(layer, n))
                dve.wait_ge(*products_done(layer, up_unit + extra))
                dve.tensor_tensor(gate[:, :, :], sets[0][:, :, 0:T], scale_of(2), ALU.mult).then_inc(gate_in.sem, 1)

            def gate_rescale(layer, n):
                dve.wait_ge(*silu_done(layer, n + 1))
                dve.tensor_tensor(gate[:, :, :], gate[:, :, :], scale_of(2), ALU.mult).then_inc(gate_scaled.sem, 1)

            def hidden(layer, n, up_unit, extra=0):
                dve.wait_ge(*products_done(layer, up_unit + extra + 1))
                dve.wait_ge(*gate_scaled(layer, n + 1))
                dve.wait_ge(*h_ready(layer, n))
                dve.tensor_tensor(h_wide[:, :, :], gate[:, :, :], sets[1][:, :, 0:T], ALU.mult).then_inc(h_full.sem, 1)

            def hidden_low(layer, n, pair_index):
                dve.wait_ge(*h_high(layer, n + 1))
                dst = bass.ds(pair_index * 2, 2)
                dve.tensor_tensor(h_lo[:, dst, :], h_wide[:, :, :], h_hi[:, dst, :].bitcast(fp32), ALU.subtract).then_inc(h_ready.sem, 1)

            def ffn(layer, first, f):
                with dve.Fori(0, (PAIRS - 1) // 2) as i:
                    for j in range(2):
                        v = first + 2 * (j + 1)
                        gate_take(layer, f, f * PAIRS + i * 2 + j, v - 1, i * 4)
                        low(layer, v, extra=i * 4)
                        gate_rescale(layer, f * PAIRS + i * 2 + j)
                        hidden(layer, f * PAIRS + i * 2 + j, v - 1, i * 4)
                        low(layer, v + 1, extra=i * 4)
                        hidden_low(layer, f * PAIRS + i * 2 + j, i * 2 + j)
                down = first + 2 * PAIRS
                gate_take(layer, f, f * PAIRS + PAIRS - 1, down - 1)
                low(layer, down)
                gate_rescale(layer, f * PAIRS + PAIRS - 1)
                hidden(layer, f * PAIRS + PAIRS - 1, down - 1)
                low(layer, down + 1)
                hidden_low(layer, f * PAIRS + PAIRS - 1, PAIRS - 1)
                low(layer, down + 2)
                low(layer, down + 3)
                n = 1 if f == 0 else 3
                for g in range(1, 4):
                    low(layer, down + 4 * g)
                    residual(layer, n, g - 1, down + 4 * g - 1, 0.5)
                    low(layer, down + 4 * g + 1)
                    u_lower(layer, n, g - 1)
                    if g > 1:
                        add_squares(layer, n, g - 1)
                    low(layer, down + 4 * g + 2)
                    low(layer, down + 4 * g + 3)

            def level_span(layer, i):
                half = HALVES[i]
                n = T_PROMPT if half == 64 else T
                if i > 0:
                    dve.wait_ge(*pair_done(layer, 2 * i))
                b = cum[:, :, 0:n].rearrange("p h (b s i) -> p h b s i", s=2, i=half)
                s = span_h[:, :, 0:n].rearrange("p h (b s i) -> p h b s i", s=2, i=half)
                ref = b[:, :, :, 0, half - 1:half].broadcast_to([P, HEADS, n // (2 * half), half])
                dve.tensor_tensor(s[:, :, :, 1, :], b[:, :, :, 1, :], ref, ALU.subtract).then_inc(span_done.sem, 1)
                dve.tensor_tensor(s[:, :, :, 0, :], ref, b[:, :, :, 0, :], ALU.subtract).then_inc(span_done.sem, 1)

            def level_pair(layer, i):
                half = HALVES[i]
                n = T_PROMPT if half == 64 else T
                dve.wait_ge(*span_exp(layer, i + 1))
                if i > 0:
                    dve.wait_ge(*level_done(layer, i))
                if i > 1:
                    dve.wait_ge(*level_kept(layer, 2 * i - 2))
                for side, src in ((1, q_gla), (0, k_gla)):
                    def halves(t):
                        return t[:, :, 0:n].rearrange("p h (b s i) -> p h b s i", s=2, i=half)[:, :, :, side, :]
                    dve.tensor_tensor(halves(pair), halves(src), halves(span_h), ALU.mult).then_inc(pair_done.sem, 1)

            def level_keep(layer, i):
                half = HALVES[i]
                n = T_PROMPT if half == 64 else T
                for j in range(2):
                    out = sT[:, 2 * j:2 * j + 2, 0:n].rearrange("p h (b s i) -> p h b s i", s=2, i=half)[:, :, :, 1, :]
                    src = aux[:, 2 * (i % 2) + j, 0:n].rearrange("p (h b i) -> p h b i", h=2, i=half)
                    m = masks[:, i, 0:n // 2].bitcast(u16).rearrange("p (o b i) -> p o b i", o=1, i=half)
                    dve.copy_predicated(out, m.broadcast_to([P, 2, n // (2 * half), half]), src).then_inc(level_kept.sem, 1)

            def gla_take(layer, r):
                dve.wait_ge(*gla_out(layer, r + 1))
                if r == 0:
                    dve.wait_ge(*last_exp(layer, 1))
                dve.tensor_copy(o_gla[:, 4 * r:4 * r + 4, :], aux[:, :, 0:T]).then_inc(gla_kept.sem, 1)

            def state_update(layer, t):
                s = (s_prompt, s_sample)[t]
                dve.wait_ge(*state_sum(layer, 2 + t))
                for h in range(HEADS):
                    dve.scalar_tensor_tensor(out=s[:, h, :], in0=s[:, h, :], scalar=last_decay[:, h, t:t + 1],
                                             in1=aux[:, 2 * t + h // 2, (h % 2) * DV:(h % 2 + 1) * DV],
                                             op0=ALU.mult, op1=ALU.add).then_inc(state_new.sem, 1)

            def attend(layer, w):
                if w == 2:
                    dve.memset(k_flat[:, HEADS * T:], 0.0).then_inc(pads_cleared.sem, 1)
                    dve.memset(pair_flat[:, HEADS * T:], 0.0).then_inc(pads_cleared.sem, 1)
                    dve.wait_ge(*logits(layer, 1))
                    for h in range(HEADS):
                        dve.tensor_scalar(span_h[:, h, :], aux[:, h, 0:T], vec[:, bass.ds(layer * VECS + B_DECAY + h, 1)], None,
                                          ALU.add).then_inc(logit_full.sem, 1)
                    dve.wait_ge(*logit_full(layer, HEADS))
                    dve.wait_ge(*logit_abs(layer, 1))
                    dve.tensor_scalar(span[:, :], span[:, :], 0.0, None, ALU.min).then_inc(logit_floor.sem, 1)
                if w == 3:
                    dve.wait_ge(*logit_floor(layer, 1))
                    dve.wait_ge(*logit_log(layer, 1))
                    for h in range(HEADS):
                        for t0, t1 in ((0, P), (P, 2 * P), (2 * P, T)):
                            dve.tensor_tensor_scan(cum[:, h, t0:t1], span_h[:, h, t0:t1], pair[:, h, t0:t1], 0.0,
                                                   ALU.add, ALU.subtract).then_inc(cum_done.sem, 1)
                    dve.wait_ge(*cum_done(layer, 3 * HEADS))
                    level_span(layer, 0)
                if w == 5:
                    dve.wait_ge(*mix_kept(layer, kept_by(FIRST["qa"] + 1)))
                    level_pair(layer, 0)
                    level_span(layer, 1)
                if w == 6:
                    dve.copy_predicated(sT[:, :, :], diag[:, :].bitcast(u16).rearrange("p (o t) -> p o t", o=1).broadcast_to([P, HEADS, T]),
                                        aux[:, :, 0:T]).then_inc(diag_kept.sem, 1)
                    dve.wait_ge(*diag_kept(layer, 1))
                if 7 <= w <= 6 + len(HALVES):
                    i = w - 7
                    if i + 1 < len(HALVES):
                        level_pair(layer, i + 1)
                        level_keep(layer, i)
                    if i + 2 < len(HALVES):
                        level_span(layer, i + 2)
                if w == 13:
                    dve.wait_ge(*carry_exp(layer, 1))
                    dve.wait_ge(*level_done(layer, len(HALVES)))
                    dve.wait_ge(*level_kept(layer, 2 * len(HALVES) - 2))
                    dve.tensor_tensor(pair[:, :, P:T], q_gla[:, :, P:T], span_h[:, :, P:T], ALU.mult).then_inc(q_carried.sem, 1)
                    dve.wait_ge(*q_carried(layer, 1))
                    b = cum[:, :, 0:2 * P].rearrange("p h (t i) -> p h t i", i=P)
                    s = span_h[:, :, 0:2 * P].rearrange("p h (t i) -> p h t i", i=P)
                    dve.tensor_tensor(s, b[:, :, :, P - 1:P].broadcast_to([P, HEADS, 2, P]), b, ALU.subtract).then_inc(key_span.sem, 1)
                    dve.tensor_tensor(span_h[:, :, 2 * P:T], cum[:, :, T - 1:T].broadcast_to([P, HEADS, T - 2 * P]),
                                      cum[:, :, 2 * P:T], ALU.subtract).then_inc(key_span.sem, 1)
                    level_keep(layer, len(HALVES) - 1)
                    dve.wait_ge(*key_exp(layer, 1))
                    dve.tensor_tensor(span_h[:, :, :], span_h[:, :, :], k_gla[:, :, :], ALU.mult).then_inc(k_carried.sem, 1)
                if w == 14:
                    dve.wait_ge(*keys_turned(layer, 1))
                    dve.tensor_copy(k_rows[0:T_SAMPLE, 2, :], aux[0:T_SAMPLE, 2, :]).then_inc(keys_tail.sem, 1)
                if w in (15, 16):
                    r = w - 15
                    dve.wait_ge(*gla_kept(layer, r + 1))
                    dve.wait_ge(*gla_root(layer, r + 1))
                    dve.reciprocal(wide[:, :, :], wide[:, :, :]).then_inc(gla_scale.sem, 1)
                    dve.wait_ge(*gla_scale(layer, r + 1))
                    for c in range(4):
                        o = o_gla[:, 4 * r + c, :]
                        dve.scalar_tensor_tensor(out=o, in0=o, scalar=vec[:, bass.ds(layer * VECS + G_GLA + 4 * r + c, 1)],
                                                 in1=wide[:, c // 2, :], op0=ALU.mult, op1=ALU.mult).then_inc(gla_norm.sem, 1)
                if w == 17:
                    state_update(layer, 1)
                    dve.tensor_copy(vs_shift[0:64, 0, :], vs[64:P, 0, :]).then_inc(v_shifted.sem, 1)
                    dve.tensor_copy(vs_shift[64:P, 0, :], vs[0:64, 1, :]).then_inc(v_shifted.sem, 1)
                    dve.tensor_copy(vs_shift[0:64, 1, :], vs[64:P, 1, :]).then_inc(v_shifted.sem, 1)
                if 18 <= w <= 25:
                    c = w - 18
                    dve.wait_ge(*scores_done(layer, c + 1))
                    for hi, c0, c1, col in PIECES:
                        dve.tensor_reduce(row_max[0:hi, :, col:col + 1], aux[0:hi, 0:2, c0:c1], AX.X, ALU.max).then_inc(max_done.sem, 1)
                    dve.wait_ge(*max_done(layer, 3 * c + 3))
                    if c > 0:
                        dve.wait_ge(*probs_done(layer, 6 * c))
                    dve.scalar_tensor_tensor(out=shift[:, :, :], in0=row_max[:, :, :], scalar=-HD ** -0.5, in1=minus_sink(layer, c),
                                             op0=ALU.mult, op1=ALU.min).then_inc(shift_done.sem, 1)
                    dve.wait_ge(*shift_done(layer, c + 1))
                    dve.tensor_tensor(sink_d[:, :, :], shift[:, :, :], minus_sink(layer, c), ALU.subtract).then_inc(sink_diff.sem, 1)

            def minus_sink(layer, c):
                return nsink[:, bass.ds(layer * 16 + 2 * c, 2)].rearrange("p (e o) -> p e o", o=1).broadcast_to([P, 2, 3])

            def soften(layer, c):
                dve.wait_ge(*probs_done(layer, 6 * c + 6))
                dve.wait_ge(*sink_exp(layer, c + 1))
                dve.tensor_tensor(den[:, :, :], sums[:, :, :], sink_d[:, :, :], ALU.add).then_inc(den_done.sem, 1)
                dve.wait_ge(*den_done(layer, c + 1))
                dve.reciprocal(den[:, :, :], den[:, :, :]).then_inc(recip_done.sem, 1)
                dve.wait_ge(*recip_done(layer, c + 1))
                for hi, c0, c1, col in PIECES:
                    pr = probs[c % 2][0:hi, :, c0:c1]
                    dve.tensor_tensor(pr, pr, den[0:hi, :, col:col + 1].broadcast_to([hi, 2, c1 - c0]), ALU.mult).then_inc(scaled.sem, 1)

            def keep(layer, w):
                kind = KIND[w]
                i = NTH[w]
                src = sets[SET[w]]
                if kind in ("va", "vb"):
                    return
                dve.wait_ge(*products_done(layer, W_MIX + w + 1))
                if w == 0:
                    dve.wait_ge(*norm_scale(layer, 2))
                if kind == "rank":
                    dve.tensor_tensor(rank, aux[0:RANK, 3, 0:T], scale[0:RANK, :], ALU.mult).then_inc(rank_kept.sem, 1)
                elif kind == "kb":
                    for odd in range(2):
                        for dst in range(2):
                            dve.tensor_tensor(kd[64 * dst:64 * dst + 64, odd:KVH:2, 0:T], src[64 * odd:64 * odd + 64, :, 0:T],
                                              scale_of(2)[64 * odd:64 * odd + 64], ALU.mult).then_inc(kb_kept.sem, 1)
                else:
                    two = slice(2 * i, 2 * i + 2)
                    if kind == "ga" and i == 0:
                        dve.wait_ge(*k_carried(layer, 1))
                    if kind == "ra" and i > 0:
                        dve.wait_ge(*ra_read(layer, i))
                    if kind == "gb" and i == 0:
                        dve.wait_ge(*state_sum(layer, 3))
                    if kind in ("qa", "ra"):
                        dve.scalar_tensor_tensor(out=q_gla[:, two, :] if kind == "qa" else sq[:, :, :], in0=src[:, :, 0:T],
                                                 scalar=DK ** -0.5 if kind == "qa" else 0.25, in1=scale_of(2),
                                                 op0=ALU.mult, op1=ALU.mult).then_inc(mix_kept.sem, 1)
                    else:
                        dst = {"ka": k_gla, "qb": qs, "ga": gate_a, "gb": gate_b}[kind]
                        dve.tensor_tensor(dst[:, two, :], src[:, :, 0:T], scale_of(2), ALU.mult).then_inc(mix_kept.sem, 1)
                if kind == "ra":
                    dve.wait_ge(*ra_tanh(layer, i + 1))
                    dve.scalar_tensor_tensor(out=wide[:, :, :], in0=wide[:, :, :], scalar=1.0, in1=sq[:, :, :],
                                             op0=ALU.add, op1=ALU.mult).then_inc(ra_read.sem, 1)
                    dve.wait_ge(*ra_read(layer, i + 1))
                    dve.wait_ge(*gate_tanh(layer, i + 1))
                    g = gate_a[:, two, :]
                    dve.scalar_tensor_tensor(out=g, in0=g, scalar=1.0, in1=wide[:, :, :], op0=ALU.add, op1=ALU.mult).then_inc(ra_gate.sem, 1)

            def merge(layer, i):
                two = slice(2 * i, 2 * i + 2)
                dve.wait_ge(*gate_b_tanh(layer, i + 1))
                dve.wait_ge(*heads_kept(layer, 2 * i + 2))
                g = gate_b[:, two, :]
                dve.scalar_tensor_tensor(out=g, in0=g, scalar=1.0, in1=qs[:, two, :], op0=ALU.add, op1=ALU.mult).then_inc(ob_gated.sem, 1)
                dve.wait_ge(*ob_gated(layer, i + 1))
                dve.wait_ge(*oa_gated(layer, i + 1))
                dve.scalar_tensor_tensor(out=wide[:, :, :], in0=g, scalar=0.5, in1=o_gla[:, two, :],
                                         op0=ALU.mult, op1=ALU.add).then_inc(merged_wide.sem, 1)

            def merged_lower(layer, i):
                dve.wait_ge(*merged_high(layer, i + 1))
                cols = slice(2 * i * T, 2 * (i + 1) * T)
                dve.tensor_tensor(merged_lo[:, cols], wide[:, :, :].rearrange("p c t -> p (c t)"), merged_hi[:, cols].bitcast(fp32),
                                  ALU.subtract).then_inc(merged_ready.sem, 1)

            dve.memset(wide[:, 0, 0:1], 0.0).then_inc(products_done.sem, SPLIT_SLOTS)
            dve.memset(wide[:, 0, 4:5], 0.0).then_inc(split_done.sem, RAW_SLOTS)
            dve.memset(wide[:, 0, 1:2], 0.0).then_inc(h_full.sem, 1)
            dve.memset(wide[:, 0, 2:3], 0.0).then_inc(h_ready.sem, 1)
            dve.memset(u_hi[:, KD_ * T:].bitcast(fp32), 0.0).then_inc(vec_init.sem, 1)
            dve.memset(u_lo[:, KD_ * T:].bitcast(fp32), 0.0).then_inc(vec_init.sem, 1)
            dve.memset(sq_sum[:, T:], 1.0).then_inc(vec_init.sem, 1)
            dve.memset(vec[:, DEPTH * VECS:], 1.0).then_inc(vec_init.sem, 1)
            low(0, U1)
            dve.wait_ge(x_loaded.sem, 32)
            dve.memset(wide[:, 0, 3:4], 0.0).then_inc(x_ready.sem, 4)
            for g in (1, 2, 3):
                u_lower(0, 0, g - 1)
                dve.wait_ge(sq_ready.sem, g + 1)
                if g > 1:
                    dve.wait_ge(acc_ready.sem, g - 1)
                dve.tensor_tensor(sq_acc[:, :, :], sq_acc[:, :, :], sq[:, :, :], ALU.add).then_inc(acc_ready.sem, 1)
            dve.wait_ge(acc_ready.sem, 3)
            dve.tensor_tensor(sq_sum[:, 0:T], sq_acc[:, 0, :], sq_acc[:, 1, :], ALU.add).then_inc(sum_ready.sem, 1)
            dve.wait_ge(loaded.sem, 32)
            dve.tensor_scalar(nsink[:, :], nsink[:, :], -1.0, None, ALU.mult).then_inc(vec_init.sem, 1)
            with dve.Fori(0, DEPTH) as layer:
                u_lower(layer, 0, 3)
                low(layer, U1 + 1)
                norm(layer, 0)
                ffn(layer, U1, 0)
                low(layer, W_MIX)
                residual(layer, 1, 3, W_MIX - 1, 0.5)
                u_lower(layer, 1, 3)
                add_squares(layer, 1, 3)
                dve.wait_ge(consts.sem, N_CONSTS)
                dve.wait_ge(vec_init.sem, 5)
                for w in range(len(MIX)):
                    if w in (15, 16):
                        gla_take(layer, w - 15)
                    if w == 17:
                        state_update(layer, 0)
                        dve.wait_ge(*state_new(layer, HEADS))
                        dve.memset(aux[0:64, 0:2, 64:P], -1e30).then_inc(band_closed.sem, 1)
                    if w == 6:
                        dve.wait_ge(*diag_done(layer, 1))
                    if w >= 18:
                        attend(layer, w)
                        low(layer, W_MIX + w + 1)
                        keep(layer, w - 1)
                    elif w == 17:
                        low(layer, W_MIX + w + 1)
                        keep(layer, w - 1)
                        attend(layer, w)
                    elif w > 1:
                        keep(layer, w - 1)
                        if w in (15, 16):
                            dve.wait_ge(*gla_sq(layer, w - 14))
                            dve.tensor_tensor(span_h[:, 0:4:2, :], span_h[:, 0:4:2, :], span_h[:, 1:4:2, :],
                                              ALU.add).then_inc(gla_sq_sum.sem, 1)
                        low(layer, W_MIX + w + 1)
                        attend(layer, w)
                    else:
                        low(layer, W_MIX + w + 1)
                    if w == 1:
                        norm(layer, 1)
                        keep(layer, 0)
                    if w >= 24:
                        merge(layer, w - 24)
                    if 18 <= w <= 25:
                        soften(layer, w - 18)
                    if w >= 24:
                        merged_lower(layer, w - 24)
                keep(layer, len(MIX) - 1)
                merge(layer, 3)
                merged_lower(layer, 3)
                dve.wait_ge(*stored(layer, 128))
                low(layer, W_OUT + 1)
                for j in range(4):
                    residual(layer, 2, j, W_OUT + j, 1.0)
                    if j < 3:
                        low(layer, W_OUT + j + 2)
                    u_lower(layer, 2, j)
                    if j > 0:
                        add_squares(layer, 2, j)
                low(layer, U2 + 1)
                norm(layer, 2)
                ffn(layer, U2, 1)
                dve.wait_ge(*pe_high(layer, 1))
                dve.tensor_tensor(pe_lo[:, :, :], pe_raw[:, :, :], pe_hi[:, :, :].bitcast(fp32), ALU.subtract).then_inc(pe_ready.sem, 1)
                low(layer, W_PLE)
                residual(layer, 3, 3, W_PLE - 1, 0.5)
                u_lower(layer, 3, 3)
                add_squares(layer, 3, 3)
                low(layer, W_PG)
                low(layer, W_PG + 1)
                norm(layer, 3)
                for j in range(4):
                    dve.wait_ge(*norm_scale(layer, 4))
                    dve.wait_ge(*products_done(layer, W_PG + j + 1))
                    if j > 0:
                        dve.wait_ge(*pg_prod(layer, j))
                    dve.tensor_tensor(gate[:, :, :], sets[j % 2][:, :, 0:T], scale_of(2), ALU.mult).then_inc(pg_in.sem, 1)
                    if j == 3:
                        u_lower(layer, 4, 0)
                        add_squares(layer, 4, 2)
                    else:
                        low(layer, W_PG + j + 2)
                    dve.wait_ge(*pg_gate(layer, j + 1))
                    dve.wait_ge(*ple_kept(layer, j + 1))
                    e = ple[:, 2 * j:2 * j + 2, :]
                    dve.tensor_tensor(e, e, gate[:, :, :], ALU.mult).then_inc(pg_prod.sem, 1)
                    dve.wait_ge(*pg_prod(layer, j + 1))
                    xs = x[:, 2 * j:2 * j + 2, :]
                    dve.tensor_tensor(xs, xs, e, ALU.add).then_inc(x_ready.sem, 1)
                    if j == 3:
                        u_lower(layer, 4, 1)
                    if j in (1, 3):
                        add_squares(layer, 4, j)
                    if j == 3:
                        u_lower(layer, 4, 2)
            dve.wait_ge(final_root.sem, 1)
            dve.reciprocal(scale[:, :], scale[:, :]).then_inc(final_scale.sem, 1)
            dve.wait_ge(final_scale.sem, 1)
            for c in range(KD_):
                dve.scalar_tensor_tensor(out=x[:, c, :], in0=x[:, c, :], scalar=gfin[:, c:c + 1], in1=scale[:, :],
                                         op0=ALU.mult, op1=ALU.mult).then_inc(y_done.sem, 1)

        @block.tensor
        def _(pe):
            def product(out, lhs_hi, lhs_lo, rhs_hi, rhs_lo, start, stop):
                pe.matmul(out, lhs_hi, rhs_hi, start=start, stop=False)
                pe.matmul(out, lhs_hi, rhs_lo, start=False, stop=False)
                return pe.matmul(out, lhs_lo, rhs_hi, start=False, stop=stop)

            def unit(layer, v, dst, hi, lo, n_k=KD_, chunks=2, first=True, last=True, extra=0, before=None, middle=None, middle_k=KD_ // 2, cols=COLS):
                pe.wait_ge(*split_done(layer, v + extra + 1))
                s = v % SPLIT_SLOTS
                for k in range(n_k):
                    if before is not None:
                        before(k)
                    if middle is not None and k == middle_k:
                        middle()
                    for m in range(chunks):
                        w = slice(k * cols + m * P, k * cols + (m + 1) * P)
                        mm = product(dst(m), w_hi[s][:, w], w_lo[s][:, w], hi(k), lo(k),
                                     first and k == 0, last and k == n_k - 1)
                mm.then_inc(products_done.sem, 1)

            def unit_by_token(layer, v, dst, middle=None):
                pe.wait_ge(*split_done(layer, v + 1))
                s = v % SPLIT_SLOTS
                for t in range(3):
                    if middle is not None and t == 1:
                        middle()
                    out = dst[:, 0, t * COLS:(t + 1) * COLS] if t < 2 else dst[:, 1, 0:COLS]
                    for k in range(KD_):
                        tok = slice(k * T + t * P, k * T + (t + 1) * P)
                        w = slice(k * COLS, (k + 1) * COLS)
                        mm = product(out, u_hi[:, tok], u_lo[:, tok], w_hi[s][:, w], w_lo[s][:, w], k == 0, k == KD_ - 1)
                mm.then_inc(products_done.sem, 1)

            def u_of(t):
                return lambda k: t[:, k * T:(k + 1) * T]

            def into(n):
                return lambda m: sets[n][:, m, 0:T]

            def norm(layer, n):
                pe.wait_ge(*sum_ready(layer, n))
                if n == 1:
                    for t in range(3):
                        pe.matmul(aux[:, 1, t:t + 1], sq_sum[:, t * P:(t + 1) * P], ones[:, 0:1], start=True, stop=True)
                pe.matmul(aux[:, 0, 0:T], ones[:, :], sq_sum[:, 0:T], start=True, stop=True).then_inc(norm_sum.sem, 1)

            def fresh_u(layer, n):
                return lambda k: pe.wait_ge(*u_ready(layer, 8 * n + k + 1))

            def ffn(layer, first, f, n_u):
                for j in range(2):
                    pe.wait_ge(*x_ready(layer, 4 * n_u - 1 + j))
                    unit(layer, first + j, into(j), u_of(u_hi), u_of(u_lo), before=fresh_u(layer, n_u) if j == 0 else None)
                    if j == 0:
                        if f == 0:
                            pe.wait_ge(consts.sem, 1)
                        norm(layer, n_u)
                with pe.Fori(1, PAIRS) as p:
                    pe.wait_ge(*gate_in(layer, f * PAIRS + p))
                    unit(layer, first, into(0), u_of(u_hi), u_of(u_lo), extra=p * 2)
                    pe.wait_ge(*h_full(layer, f * PAIRS + p))
                    unit(layer, first + 1, into(1), u_of(u_hi), u_of(u_lo), extra=p * 2)
                down = first + 2 * PAIRS
                n = 1 if f == 0 else 3
                with pe.Fori(0, 2) as i:
                    for b in range(2):
                        pe.wait_ge(*h_ready(layer, f * PAIRS + PAIRS - 1))
                        pe.wait_ge(*(gate_in if b == 0 else h_full)(layer, (f + 1) * PAIRS))
                        pe.wait_ge(*x_ready(layer, 4 * (n - 1) + i * 2 + b - 1))
                        for q, (k0, cnt) in enumerate(PARTS):
                            if q == 3:
                                pe.wait_ge(*h_ready(layer, (f + 1) * PAIRS))
                            unit(layer, down + 4 * b + q, into(b), lambda k: h_hi[:, k0 + k, :], lambda k: h_lo[:, k0 + k, :],
                                 n_k=cnt, first=q == 0, last=q == 3, extra=i * 8)

            def wait_kept(layer, w):
                kind = KIND[w]
                if kind == "kb":
                    pe.wait_ge(*kb_kept(layer, 4))
                elif kind in ("va", "vb"):
                    pe.wait_ge(*values_kept(layer, sum(k in ("va", "vb") for k in KIND[:w + 1])))
                else:
                    pe.wait_ge(*mix_kept(layer, kept_by(w)))

            def scores(layer, c):
                if c == 0:
                    pe.wait_ge(*state_new(layer, HEADS))
                    pe.wait_ge(*kb_kept(layer, 4))
                    pe.wait_ge(*mix_loaded(layer, 80))
                    pe.wait_ge(*mix_kept(layer, kept_by(FIRST["qb"] + 3)))
                    pe.wait_ge(*band_closed(layer, 1))
                else:
                    pe.wait_ge(*probs_done(layer, 6 * c))
                g = c // 2
                for e in range(2):
                    r = slice(64 * e, 64 * e + 64)
                    pe.matmul(aux[:, e, 0:64], qs[r, c, 0:P], kd[r, g, 0:64], start=True, stop=True)
                    pe.matmul(aux[64:P, e, 64:P], qs[r, c, 64:P], kd[r, g, 64:P], start=True, stop=True)
                    pe.matmul(aux[0:64, e, 128:320], qs[r, c, 128:192], kd[r, g, 0:192], start=True, stop=True)
                    pe.matmul(aux[64:P, e, 128:320], qs[r, c, 192:256], kd[r, g, 64:256], start=True, stop=True)
                    mm = pe.matmul(aux[0:64, e, 320:512], qs[r, c, 256:T], kd[r, g, 256:448], start=True, stop=True)
                mm.then_inc(scores_done.sem, 1)

            def turn(layer, c):
                pe.wait_ge(*scaled(layer, 3 * c + 3))
                if c == 0:
                    pe.wait_ge(*state_new(layer, 2 * HEADS))
                else:
                    pe.wait_ge(*heads_kept(layer, c))
                for e in range(2):
                    out, pr = aux[:, 2 + e, :], probs[c % 2][:, e, :]
                    pe.transpose(out[:, 0:128], pr[:, 0:128], ident[:, :])
                    pe.transpose(out[:, 128:256], pr[:, 128:256], ident[:, :])
                    pe.transpose(out[:, 256:320], pr[0:64, 384:512], ident[0:64, 0:64])
                    pe.transpose(out[0:64, 320:448], pr[:, 256:320], ident[:, :])
                    mm = pe.transpose(out[0:64, 448:512], pr[0:64, 320:384], ident[0:64, 0:64])
                mm.then_inc(turned.sem, 1)

            def heads(layer, c):
                if c == 0:
                    pe.wait_ge(*v_shifted(layer, 3))
                pe.wait_ge(*turned_kept(layer, 4 * c + 4))
                col = slice((c // 2) * HD, (c // 2 + 1) * HD)
                for e in range(2):
                    out, pt = aux[64 * e:64 * e + 64, 2, :], probs_t[:, e, :]
                    pe.matmul(out[:, 0:192], vs[:, 0, col], pt[:, 0:192], start=True, stop=False)
                    pe.matmul(out[:, 128:192], vs[0:64, 1, col], pt[0:64, 320:384], start=False, stop=True)
                    pe.matmul(out[:, 192:256], vs_shift[:, 0, col], pt[:, 192:256], start=True, stop=False)
                    pe.matmul(out[:, 192:256], vs_shift[0:64, 1, col], pt[0:64, 384:448], start=False, stop=True)
                    pe.matmul(out[:, 256:T], vcache[:, col], pt[:, 256:320], start=True, stop=False)
                    mm = pe.matmul(out[:, 256:T], vs[0:64, 2, col], pt[0:64, 448:512], start=False, stop=True)
                mm.then_inc(heads_out.sem, 1)

            def state_products(layer, t, bank):
                rows = T_SAMPLE if t == 2 else P
                for h in range(HEADS):
                    mm = pe.matmul(aux[:, bank + h // 2, (h % 2) * DV:(h % 2 + 1) * DV], k_rows[0:rows, t, h * DK:(h + 1) * DK],
                                   v_gla[0:rows, t, h * DV:(h + 1) * DV], start=True, stop=True)
                mm.then_inc(state_sum.sem, 1)

            def gla_products(layer, r):
                for n in range(4):
                    h, c0 = 2 * r + n // 2, (n % 2) * P
                    v = h * DV + c0
                    out = aux[:, n, :]
                    pe.matmul(out[:, 0:P], v_gla[:, 0, v:v + P], sT[:, h, 0:P], start=True, stop=True)
                    pe.matmul(out[:, P:2 * P], v_gla[:, 1, v:v + P], sT[:, h, P:2 * P], start=True, stop=False)
                    pe.matmul(out[:, P:2 * P], s_prompt[:, h, c0:c0 + P], pair[:, h, P:2 * P], start=False, stop=True)
                    pe.matmul(out[:, 2 * P:T], v_gla[0:64, 2, v:v + P], sT[0:64, h, 2 * P:T], start=True, stop=False)
                    mm = pe.matmul(out[:, 2 * P:T], s_sample[:, h, c0:c0 + P], pair[:, h, 2 * P:T], start=False, stop=True)
                mm.then_inc(gla_out.sem, 1)

            def gla_sums(layer, r):
                pe.wait_ge(*gla_kept(layer, r + 1))
                pe.wait_ge(*gla_sq_sum(layer, r + 1))
                for n in range(2):
                    mm = pe.matmul(aux[:, 2 * r + n, 0:T], ones[:, :], span_h[:, 2 * n, :], start=True, stop=True)
                mm.then_inc(gla_sum.sem, 1)

            def within(layer, w):
                if w == 2:
                    pe.wait_ge(*rank_kept(layer, 1))
                    pe.wait_ge(*mix_loaded(layer, 80))
                    for h in range(HEADS):
                        mm = pe.matmul(aux[:, h, 0:T], wa2[:, h * DK:(h + 1) * DK], rank, start=True, stop=True)
                    mm.then_inc(logits.sem, 1)
                if w == 14:
                    pe.wait_ge(*keys_kept(layer, 1))
                    state_products(layer, 0, 0)
                if w in (15, 16):
                    gla_sums(layer, w - 15)
                if w == 17:
                    pe.wait_ge(*gla_root(layer, 2))
                    state_products(layer, 2, 2)
                if 19 <= w <= 26:
                    turn(layer, w - 19)

            def after(layer, w):
                if w == 0:
                    norm(layer, 1)
                if w == 5:
                    pe.wait_ge(*cum_done(layer, 3 * HEADS))
                    pe.wait_ge(*pads_cleared(layer, 2))
                    pe.wait_ge(*mix_kept(layer, kept_by(FIRST["qa"] + 1)))
                    for h in range(HEADS):
                        for t, n in ((0, P), (1, P), (2, T_SAMPLE)):
                            mm = pe.matmul(aux[:, h, t * P:t * P + n], k_flat[:, h * T + t * P:h * T + (t + 1) * P],
                                           q_gla[:, h, t * P:t * P + n], start=True, stop=True)
                    mm.then_inc(diag_done.sem, 1)
                if 6 <= w <= 5 + len(HALVES):
                    i = w - 6
                    half = HALVES[i]
                    pe.wait_ge(*pair_done(layer, 2 * i + 2))
                    pe.wait_ge(*diag_kept(layer, 1))
                    if i >= 2:
                        pe.wait_ge(*level_kept(layer, 2 * i - 2))
                    tiles = ((0, P), (1, P)) if half == 64 else ((0, P), (1, P), (2, T_SAMPLE))
                    per_head = (T_PROMPT if half == 64 else T) // 2
                    for h in range(HEADS):
                        for t, n in tiles:
                            rhs = pair[:, h, t * P:t * P + n].rearrange("p (b s i) -> p b s i", s=2, i=half)[:, :, 1, :]
                            c0 = (h % 2) * per_head + t * 64
                            out = aux[:, 2 * (i % 2) + h // 2, c0:c0 + n // 2]
                            mm = pe.matmul(out.rearrange("p (b i) -> p b i", i=half), pair_flat[:, h * T + t * P:h * T + (t + 1) * P],
                                           rhs, start=True, stop=True)
                    mm.then_inc(level_done.sem, 1)
                if w == 13:
                    pe.wait_ge(*k_carried(layer, 1))
                    pe.wait_ge(*level_kept(layer, 2 * len(HALVES)))
                    for t, n in ((0, P), (1, P), (2, T_SAMPLE)):
                        for h in range(HEADS):
                            mm = pe.transpose(aux[0:n, t, h * DK:(h + 1) * DK], span_h[:, h, t * P:t * P + n], ident[:, :])
                    mm.then_inc(keys_turned.sem, 1)
                if w == 14:
                    pe.wait_ge(*state_first(layer, 1))
                    pe.wait_ge(*keys_tail(layer, 1))
                    pe.wait_ge(*mix_loaded(layer, 80))
                    gla_products(layer, 0)
                if w == 15:
                    pe.wait_ge(*gla_root(layer, 1))
                    gla_products(layer, 1)
                if w == 16:
                    state_products(layer, 1, 0)
                if 17 <= w <= 24:
                    scores(layer, w - 17)
                if 19 <= w <= 26:
                    heads(layer, w - 19)

            pe.wait_ge(vec_init.sem, 4)
            with pe.Fori(0, DEPTH) as layer:
                ffn(layer, U1, 0, 0)
                pe.wait_ge(consts.sem, N_CONSTS)
                for w, kind in enumerate(KIND):
                    v = W_MIX + w
                    if w >= 4:
                        wait_kept(layer, w - 2)
                    elif w == 3:
                        wait_kept(layer, 0)
                    elif kind != "rank":
                        pe.wait_ge(*x_ready(layer, 3 + SET[w]))
                    if kind == "rank":
                        unit(layer, v, lambda m: aux[:, 3, 0:T], u_of(u_hi), u_of(u_lo), chunks=1, cols=P)
                    elif kind in ("va", "vb"):
                        unit_by_token(layer, v, sets[SET[w]], middle=lambda: within(layer, w))
                    else:
                        unit(layer, v, into(SET[w]), u_of(u_hi), u_of(u_lo), middle=lambda: within(layer, w),
                             middle_k=5 if w in (15, 16) else 4,
                             before=fresh_u(layer, 1) if w == 0 else None)
                    after(layer, w)

                def fresh_merged(k):
                    if k % 2 == 0:
                        pe.wait_ge(*merged_ready(layer, k // 2 + 1))
                for j in range(4):
                    if j < 2:
                        wait_kept(layer, len(MIX) - 2 + j)
                    else:
                        pe.wait_ge(*x_ready(layer, 4 + j - 1))
                    unit(layer, W_OUT + j, into(j % 2), u_of(merged_hi), u_of(merged_lo), before=fresh_merged if j == 0 else None)
                ffn(layer, U2, 1, 2)
                pe.wait_ge(*split_done(layer, W_PLE + 1))
                pe.wait_ge(*pe_ready(layer, 1))
                s = W_PLE % SPLIT_SLOTS
                for c in range(4):
                    if c == 0:
                        pe.wait_ge(*x_ready(layer, 8 + 3))
                    if c == 3:
                        pe.wait_ge(*x_ready(layer, 8 + 4))
                    dst = ple_place[c]
                    for m in range(2):
                        for k in range(2):
                            w = slice(k * D + (2 * c + m) * P, k * D + (2 * c + m + 1) * P)
                            mm = product(dst[:, m, 0:T], w_hi[s][:, w], w_lo[s][:, w], pe_hi[:, k, :], pe_lo[:, k, :], k == 0, k == 1)
                    mm.then_inc(products_done.sem if c == 3 else ple_done.sem, 1)
                pe.wait_ge(*ple_kept(layer, 3))
                norm(layer, 3)
                for j in range(4):
                    if j < 2:
                        pe.wait_ge(*ple_kept(layer, 3 * j + 1))
                    else:
                        pe.wait_ge(*pg_in(layer, j - 1))
                    unit(layer, W_PG + j, into(j % 2), u_of(u_hi), u_of(u_lo), before=fresh_u(layer, 3) if j == 0 else None)
            pe.wait_ge(sum_ready.sem, 1 + 4 * DEPTH)
            pe.matmul(aux[:, 0, 0:T], ones[:, :], sq_sum[:, 0:T], start=True, stop=True).then_inc(final_sum.sem, 1)


def kernel(**inputs):
    import numpy as np
    import concourse.bacc as bacc
    from concourse.bass_utils import run_bass_kernel_spmd as run

    a = {k: np.asarray(v) for k, v in inputs.items()}

    def chunks(v):
        return np.moveaxis(v.reshape(*v.shape[:-1], -1, P), -1, -2)

    def columns(prompt, sample):
        both = np.concatenate([prompt, sample], axis=-2)
        return np.moveaxis(chunks(both), -3, -1)

    ins = {
        "xT": columns(a["x_prompt"][0], a["x_sample"][0]),
        "peT": columns(a["p_prompt"][:, 0], a["p_sample"][:, 0]),
        "kcT": np.moveaxis(a["cache_swa_k"][:, 0], 1, 3).swapaxes(1, 2),
        "vc": a["cache_swa_v"].reshape(DEPTH, CACHE, KVH * HD),
        "s0": a["state_gla"][:, 0],
        "vecs": np.concatenate([chunks(a[k]) for k in ("g_ffn1", "g_mix", "g_ffn2", "g_ple", "g_gla", "b_gla_a")], axis=-1),
        "g_final": chunks(a["g_final"]),
        "sinks": a["swa_sinks"],
        "w_up1": a["w_ffn1_up"], "w_down1": a["w_ffn1_down"], "w_in": a["w_in"], "w_a2": a["w_gla_a2"], "w_out": a["w_out"],
        "w_up2": a["w_ffn2_up"], "w_down2": a["w_ffn2_down"], "w_pg": a["w_ple_gate"], "w_ple": a["w_ple"],
    }
    outs = {
        "yT": (P, KD_, T), "pk": (DEPTH, HD, KVH, P), "pv": (DEPTH, P, KVH * HD), "pstate": (DEPTH, HEADS, DK, DV),
        "sk": (DEPTH, HD, KVH, CACHE), "sv": (DEPTH, CACHE, KVH * HD), "sstate": (DEPTH, HEADS, DK, DV),
    }
    nc = bacc.Bacc("TRN2", target_bir_lowering=False, num_devices=1)
    arrays, aps = {}, []
    for name, v in ins.items():
        v = np.ascontiguousarray(v)
        arrays[name] = v
        aps.append(nc.dram_tensor(name, v.shape, mybir.dt.from_np(v.dtype), kind="ExternalInput").ap())
    for name, shape in outs.items():
        aps.append(nc.dram_tensor(name, shape, mybir.dt.float32, kind="ExternalOutput").ap())
    trunk_kernel(nc, *aps)
    got = run(nc, [arrays], core_ids=[0]).results[0]

    y = np.moveaxis(got["yT"], 2, 0).swapaxes(1, 2).reshape(T, D)
    keys = lambda k: np.moveaxis(got[k], 3, 1).swapaxes(2, 3).reshape(DEPTH, 1, P, KVH, HD)
    values = lambda k: got[k].reshape(DEPTH, 1, P, KVH, HD)
    state = lambda k: got[k].reshape(DEPTH, 1, HEADS, DK, DV)
    return (np.ascontiguousarray(y[None, :T_PROMPT]), np.ascontiguousarray(y[None, T_PROMPT:]),
            np.ascontiguousarray(keys("pk")), values("pv"), state("pstate"),
            np.ascontiguousarray(keys("sk")), values("sv"), state("sstate"))
```
